# Optimizing a Trainium2 kernel written in Bass

```python
import jax, jax.numpy as jnp
from jax import lax
import numpy as np
import jax
import jax.numpy as jnp

D_MODEL = 1024
BATCH = 1
SEQ = 512
DEPTH = 1

CONV_WIDTH = D_MODEL
CONV_K = 3
HEAD_DIM = 64
N_Q_HEADS = 8
N_KV_HEADS = 2
GQA_GROUP = N_Q_HEADS // N_KV_HEADS
WINDOW = 128
BLOCK = WINDOW
ROPE_THETA = 10000.0
Q_WIDTH = N_Q_HEADS * HEAD_DIM
KV_WIDTH = N_KV_HEADS * HEAD_DIM
D_FF = 2816
FFN_CONV_K = 3
EPS = 1e-5

IN_SIZES = (CONV_WIDTH, CONV_WIDTH, CONV_WIDTH, Q_WIDTH, KV_WIDTH, KV_WIDTH, D_MODEL, D_MODEL)
IN_WIDTH = sum(IN_SIZES)
IN_SPLITS = tuple(int(c) for c in np.cumsum(IN_SIZES)[:-1])


def rmsnorm(x, w):
    xf = x.astype(jnp.float32)
    xf = xf * lax.rsqrt(jnp.mean(xf * xf, axis=-1, keepdims=True) + EPS)
    return xf.astype(x.dtype) * w

def causal_dwconv(v, w, b=None):
    k_taps = w.shape[0]
    s = v.shape[1]
    vp = jnp.pad(v, ((0, 0), (k_taps - 1, 0), (0, 0)))
    y = sum(w[i] * vp[:, i:i + s] for i in range(k_taps))
    if b is not None:
        y = y + b
    return y

def rope_tables(positions, dtype):
    inv_freq = ROPE_THETA ** (-jnp.arange(0, HEAD_DIM, 2, dtype=jnp.float32) / HEAD_DIM)
    ang = positions.astype(jnp.float32)[..., None] * inv_freq
    return jnp.cos(ang)[:, :, None, :].astype(dtype), jnp.sin(ang)[:, :, None, :].astype(dtype)

def apply_rope(x, cos, sin):
    x1, x2 = jnp.split(x, 2, axis=-1)
    return jnp.concatenate([x1 * cos - x2 * sin, x2 * cos + x1 * sin], axis=-1)

def sliding_window_attention(q, k, v, sinks):
    b, s = q.shape[:2]
    nb = s // BLOCK
    qb = q.reshape(b, nb, BLOCK, N_KV_HEADS, GQA_GROUP, HEAD_DIM)

    def with_prev(t):
        tb = t.reshape(b, nb, BLOCK, N_KV_HEADS, HEAD_DIM)
        prev = jnp.pad(tb[:, :-1], ((0, 0), (1, 0), (0, 0), (0, 0), (0, 0)))
        return jnp.concatenate([prev, tb], axis=2)

    kk, vv = with_prev(k), with_prev(v)
    scale = HEAD_DIM ** -0.5
    scores = jnp.einsum('bnqhgd,bnkhd->bnhgqk', qb, kk).astype(jnp.float32) * scale

    q_pos = jnp.arange(BLOCK)[:, None] + BLOCK
    k_pos = jnp.arange(2 * BLOCK)[None, :]
    rel = q_pos - k_pos
    band = (rel >= 0) & (rel < WINDOW)
    not_pad = (jnp.arange(nb)[:, None, None] > 0) | (k_pos[None] >= BLOCK)
    valid = band[None] & not_pad
    scores = jnp.where(valid[None, :, None, None], scores, -jnp.inf)

    sink = sinks.astype(jnp.float32).reshape(N_KV_HEADS, GQA_GROUP)[None, None, :, :, None, None]
    m = jnp.maximum(jnp.max(scores, axis=-1, keepdims=True), sink)
    p = jnp.exp(scores - m)
    denom = jnp.sum(p, axis=-1, keepdims=True) + jnp.exp(sink - m)
    probs = (p / denom).astype(v.dtype)
    out = jnp.einsum('bnhgqk,bnkhd->bnqhgd', probs, vv)
    return out.reshape(b, s, Q_WIDTH)

def first_inputs(seed: int = 0) -> dict:
    key = jax.random.key(seed)
    ks = jax.random.split(key, 20)
    f32 = jnp.float32

    def nrm(k, shape, scale):
        return jax.random.normal(k, shape, f32) * scale

    x = jax.random.normal(ks[0], (BATCH, SEQ, D_MODEL), f32)
    positions = jnp.broadcast_to(jnp.arange(SEQ, dtype=jnp.int32), (BATCH, SEQ))
    return {
        "x": x,
        "positions": positions,
        "norm_mix_w": 1.0 + nrm(ks[1], (DEPTH, D_MODEL), 0.02),
        "w_in": nrm(ks[2], (DEPTH, D_MODEL, IN_WIDTH), D_MODEL ** -0.5),
        "b_in": nrm(ks[3], (DEPTH, IN_WIDTH), 0.02),
        "conv_mix_w": nrm(ks[4], (DEPTH, CONV_K, CONV_WIDTH), CONV_K ** -0.5),
        "w_conv_out": nrm(ks[5], (DEPTH, CONV_WIDTH, D_MODEL), CONV_WIDTH ** -0.5),
        "w_attn_out": nrm(ks[6], (DEPTH, Q_WIDTH, D_MODEL), Q_WIDTH ** -0.5),
        "b_attn_out": nrm(ks[7], (DEPTH, D_MODEL), 0.02),
        "sinks": nrm(ks[8], (DEPTH, N_Q_HEADS), 1.0),
        "w_mix_out": nrm(ks[9], (DEPTH, D_MODEL, D_MODEL), D_MODEL ** -0.5),
        "norm_ffn_w": 1.0 + nrm(ks[10], (DEPTH, D_MODEL), 0.02),
        "w_ffn_up": nrm(ks[11], (DEPTH, D_MODEL, 2 * D_FF), D_MODEL ** -0.5),
        "ffn_conv_w": nrm(ks[12], (DEPTH, FFN_CONV_K, D_FF), FFN_CONV_K ** -0.5),
        "ffn_conv_b": nrm(ks[13], (DEPTH, D_FF), 0.02),
        "w_ffn_down": nrm(ks[14], (DEPTH, D_FF, D_MODEL), D_FF ** -0.5),
        "norm_final_w": 1.0 + nrm(ks[15], (D_MODEL,), 0.02),
    }

def first_block(x, positions, norm_mix_w, w_in, b_in, conv_mix_w, w_conv_out, w_attn_out,
              b_attn_out, sinks, w_mix_out, norm_ffn_w, w_ffn_up, ffn_conv_w, ffn_conv_b,
              w_ffn_down, norm_final_w):
    b, s, _ = x.shape
    cos, sin = rope_tables(positions, x.dtype)
    for l in range(DEPTH):
        u = rmsnorm(x, norm_mix_w[l])
        proj = u @ w_in[l] + b_in[l]
        cb, cc, cx, q, k, v, g_conv, g_attn = jnp.split(proj, IN_SPLITS, axis=-1)

        y_conv = (cb * causal_dwconv(cc * cx, conv_mix_w[l])) @ w_conv_out[l]

        q = apply_rope(q.reshape(b, s, N_Q_HEADS, HEAD_DIM), cos, sin)
        k = apply_rope(k.reshape(b, s, N_KV_HEADS, HEAD_DIM), cos, sin)
        v = v.reshape(b, s, N_KV_HEADS, HEAD_DIM)
        y_attn = sliding_window_attention(q, k, v, sinks[l]) @ w_attn_out[l] + b_attn_out[l]

        merged = jax.nn.sigmoid(g_conv) * y_conv + jax.nn.sigmoid(g_attn) * y_attn
        x = x + merged @ w_mix_out[l]

        u = rmsnorm(x, norm_ffn_w[l])
        up, gate = jnp.split(u @ w_ffn_up[l], 2, axis=-1)
        a = causal_dwconv(up, ffn_conv_w[l], ffn_conv_b[l])
        x = x + (jax.nn.silu(a) * gate) @ w_ffn_down[l]
    return rmsnorm(x, norm_final_w)


N_SB_HEADS = 8
N_FOX_HEADS = 8
SB_WIDTH = N_SB_HEADS * HEAD_DIM
FOX_WIDTH = N_FOX_HEADS * HEAD_DIM
MIX_WIDTH = SB_WIDTH + FOX_WIDTH
IN_WIDTH_2 = 3 * SB_WIDTH + 3 * FOX_WIDTH + N_FOX_HEADS
BLOCK_Q = 128
N_MOD = 9
EPS_2 = 1e-6


def rms_norm(x, gain):
    xf = x.astype(jnp.float32)
    y = xf * lax.rsqrt(jnp.mean(xf * xf, axis=-1, keepdims=True) + EPS_2)
    return (y * gain.astype(jnp.float32)).astype(x.dtype)

def modulate(h, shift, scale):
    return h * (1 + scale[:, None, :]) + shift[:, None, :]

def swiglu(h, w_gate, w_up, w_down):
    return (jax.nn.silu(h @ w_gate) * (h @ w_up)) @ w_down

def split_heads(t, n_heads):
    b, s, _ = t.shape
    return t.reshape(b, s, n_heads, HEAD_DIM).transpose(0, 2, 1, 3)

def stick_breaking_attention(q, k, v):
    seq = q.shape[2]
    scale = HEAD_DIM ** -0.5
    outs = []
    for start in range(0, seq, BLOCK_Q):
        end = start + BLOCK_Q
        z = jnp.einsum('bhqd,bhkd->bhqk', q[:, :, start:end], k[:, :, :end]).astype(jnp.float32) * scale
        mask = jnp.arange(end)[None, :] < jnp.arange(start, end)[:, None]
        log_beta = jax.nn.log_sigmoid(z)
        log_keep = jnp.where(mask, jax.nn.log_sigmoid(-z), 0.0)
        later = lax.cumsum(log_keep, axis=3, reverse=True) - log_keep
        w = jnp.where(mask, jnp.exp(log_beta + later), 0.0)
        outs.append(jnp.einsum('bhqk,bhkd->bhqd', w.astype(v.dtype), v[:, :, :end]))
    return jnp.concatenate(outs, axis=2)

def forgetting_attention(q, k, v, log_f_cum):
    seq = q.shape[2]
    scale = HEAD_DIM ** -0.5
    outs = []
    for start in range(0, seq, BLOCK_Q):
        end = start + BLOCK_Q
        z = jnp.einsum('bhqd,bhkd->bhqk', q[:, :, start:end], k[:, :, :end]).astype(jnp.float32) * scale
        z = z + log_f_cum[:, :, start:end, None] - log_f_cum[:, :, None, :end]
        mask = jnp.arange(end)[None, :] <= jnp.arange(start, end)[:, None]
        p = jax.nn.softmax(jnp.where(mask, z, -jnp.inf), axis=-1)
        outs.append(jnp.einsum('bhqk,bhkd->bhqd', p.astype(v.dtype), v[:, :, :end]))
    return jnp.concatenate(outs, axis=2)

def hybrid_mixer(h, w_in, b_f, g_q, g_k, w_o):
    proj = h @ w_in
    splits = [SB_WIDTH, 2 * SB_WIDTH, 3 * SB_WIDTH,
              3 * SB_WIDTH + FOX_WIDTH, 3 * SB_WIDTH + 2 * FOX_WIDTH, 3 * SB_WIDTH + 3 * FOX_WIDTH]
    sb_q, sb_k, sb_v, fox_q, fox_k, fox_v, fox_f = jnp.split(proj, splits, axis=-1)
    sb_out = stick_breaking_attention(split_heads(sb_q, N_SB_HEADS), split_heads(sb_k, N_SB_HEADS),
                                      split_heads(sb_v, N_SB_HEADS))
    fq = rms_norm(split_heads(fox_q, N_FOX_HEADS), g_q[None, :, None, :])
    fk = rms_norm(split_heads(fox_k, N_FOX_HEADS), g_k[None, :, None, :])
    log_f = jax.nn.log_sigmoid((fox_f + b_f).astype(jnp.float32))
    log_f_cum = jnp.cumsum(log_f, axis=1).transpose(0, 2, 1)
    fox_out = forgetting_attention(fq, fk, split_heads(fox_v, N_FOX_HEADS), log_f_cum)
    heads = jnp.concatenate([sb_out, fox_out], axis=1)
    b, _, s, _ = heads.shape
    return heads.transpose(0, 2, 1, 3).reshape(b, s, MIX_WIDTH) @ w_o

def second_inputs(seed: int = 0) -> dict:
    key = jax.random.key(seed)
    ks = jax.random.split(key, 20)
    nrm = jax.random.normal
    d_s = D_MODEL ** -0.5
    return {
        'x': nrm(ks[0], (BATCH, SEQ, D_MODEL), jnp.float32),
        'c': nrm(ks[1], (BATCH, D_MODEL), jnp.float32),
        'w_mod': nrm(ks[2], (DEPTH, D_MODEL, N_MOD * D_MODEL), jnp.float32) * (0.1 * d_s),
        'b_mod': nrm(ks[3], (DEPTH, N_MOD * D_MODEL), jnp.float32) * 0.01,
        'g_ffn1': 1.0 + 0.02 * nrm(ks[4], (DEPTH, D_MODEL), jnp.float32),
        'w1_gate': nrm(ks[5], (DEPTH, D_MODEL, D_FF), jnp.float32) * d_s,
        'w1_up': nrm(ks[6], (DEPTH, D_MODEL, D_FF), jnp.float32) * d_s,
        'w1_down': nrm(ks[7], (DEPTH, D_FF, D_MODEL), jnp.float32) * D_FF ** -0.5,
        'g_mix': 1.0 + 0.02 * nrm(ks[8], (DEPTH, D_MODEL), jnp.float32),
        'w_in': nrm(ks[9], (DEPTH, D_MODEL, IN_WIDTH_2), jnp.float32) * d_s,
        'b_f': jax.random.uniform(ks[10], (DEPTH, N_FOX_HEADS), jnp.float32, 1.0, 4.0),
        'g_q': 1.0 + 0.02 * nrm(ks[11], (DEPTH, N_FOX_HEADS, HEAD_DIM), jnp.float32),
        'g_k': 1.0 + 0.02 * nrm(ks[12], (DEPTH, N_FOX_HEADS, HEAD_DIM), jnp.float32),
        'w_o': nrm(ks[13], (DEPTH, MIX_WIDTH, D_MODEL), jnp.float32) * MIX_WIDTH ** -0.5,
        'g_ffn2': 1.0 + 0.02 * nrm(ks[14], (DEPTH, D_MODEL), jnp.float32),
        'w2_gate': nrm(ks[15], (DEPTH, D_MODEL, D_FF), jnp.float32) * d_s,
        'w2_up': nrm(ks[16], (DEPTH, D_MODEL, D_FF), jnp.float32) * d_s,
        'w2_down': nrm(ks[17], (DEPTH, D_FF, D_MODEL), jnp.float32) * D_FF ** -0.5,
    }

def second_block(x, c, w_mod, b_mod, g_ffn1, w1_gate, w1_up, w1_down, g_mix, w_in, b_f, g_q, g_k,
              w_o, g_ffn2, w2_gate, w2_up, w2_down):
    c_act = jax.nn.silu(c)
    for l in range(DEPTH):
        mod = c_act @ w_mod[l] + b_mod[l]
        sh1, sc1, ga1, sh2, sc2, ga2, sh3, sc3, ga3 = jnp.split(mod, N_MOD, axis=-1)
        h = modulate(rms_norm(x, g_ffn1[l]), sh1, sc1)
        x = x + 0.5 * (1 + ga1[:, None, :]) * swiglu(h, w1_gate[l], w1_up[l], w1_down[l])
        h = modulate(rms_norm(x, g_mix[l]), sh2, sc2)
        x = x + (1 + ga2[:, None, :]) * hybrid_mixer(h, w_in[l], b_f[l], g_q[l], g_k[l], w_o[l])
        h = modulate(rms_norm(x, g_ffn2[l]), sh3, sc3)
        x = x + 0.5 * (1 + ga3[:, None, :]) * swiglu(h, w2_gate[l], w2_up[l], w2_down[l])
    return x


def setup_inputs(seed=0):
    out = dict(first_inputs(seed))
    for name, value in second_inputs(seed + 1).items():
        if name != "x":
            out[name + "_2"] = value
    return out


def reference(
    x, positions, norm_mix_w, w_in, b_in, conv_mix_w, w_conv_out, w_attn_out, b_attn_out, sinks,
    w_mix_out, norm_ffn_w, w_ffn_up, ffn_conv_w, ffn_conv_b, w_ffn_down, norm_final_w, c_2,
    w_mod_2, b_mod_2, g_ffn1_2, w1_gate_2, w1_up_2, w1_down_2, g_mix_2, w_in_2, b_f_2, g_q_2,
    g_k_2, w_o_2, g_ffn2_2, w2_gate_2, w2_up_2, w2_down_2,
):
    x = first_block(
        x, positions, norm_mix_w, w_in, b_in, conv_mix_w, w_conv_out, w_attn_out, b_attn_out,
        sinks, w_mix_out, norm_ffn_w, w_ffn_up, ffn_conv_w, ffn_conv_b, w_ffn_down,
        norm_final_w,
    )
    return second_block(
        x, c_2, w_mod_2, b_mod_2, g_ffn1_2, w1_gate_2, w1_up_2, w1_down_2, g_mix_2, w_in_2,
        b_f_2, g_q_2, g_k_2, w_o_2, g_ffn2_2, w2_gate_2, w2_up_2, w2_down_2,
    )


_drawn_inputs = setup_inputs


def setup_inputs(seed=0):
    import zlib

    import numpy as np

    out = dict(_drawn_inputs(seed))
    spreads = {}
    factors = {'b_attn_out': 4.341,
     'sinks': 5.548,
     'norm_ffn_w': 3.777,
     'ffn_conv_b': 5.4,
     'b_mod_2': 3.639,
     'g_ffn1_2': 6.342,
     'g_mix_2': 4.565,
     'g_q_2': 8.0,
     'g_k_2': 8.0,
     'g_ffn2_2': 7.942}
    for name, (base, spread) in spreads.items():
        noise = np.random.default_rng([zlib.crc32(name.encode()), seed]).standard_normal(out[name].shape)
        drawn = base * np.exp(spread * noise) if base else spread * noise
        out[name] = jnp.asarray(drawn.astype(out[name].dtype))
    for name, factor in factors.items():
        out[name] = (out[name] * factor).astype(out[name].dtype)
    return out
```

```python
from contextlib import ExitStack, contextmanager

import numpy as np

import concourse.bass as bass
from concourse import mybir
from concourse.alu_op_type import AluOpType as ALU

ACT = mybir.ActivationFunctionType
F32 = mybir.dt.float32
F32R = mybir.dt.float32r
I32 = mybir.dt.int32
AX_X = mybir.AxisListType.X

P = 128
SEQ = 512
TB = SEQ // P
D_MODEL = 1024
KC = D_MODEL // P
HEAD_DIM = 64
D_FF = 2816
FF_TILES = D_FF // P
FF_PARTS = (8, 8, 6)
assert sum(FF_PARTS) == FF_TILES
N_SWA_HEADS = 8
IN1 = dict(cb=0, cc=1024, cx=2048, q=3072, k=3584, v=3712, gc=3840, ga=4864)
IN2 = dict(sq=0, sk=512, sv=1024, fq=1536, fk=2048, fv=2560, ff=3072)
N_FOX = 8
N_MOD = 9
EPS1 = 1e-5
EPS2 = 1e-6
MASKED = -1e30
ROPE_THETA = 10000.0
TWO_PI = 6.283185307179586
PI_A = 6.28125
PI_B = float(np.float32(TWO_PI - PI_A))
ROUND = 12582912.0
RAW_SLOTS = 4
CUT_SLOTS = 2
TRI_BANK = (0, 1, 2, 2)
TRI_COL = (0, 0, 0, 256)
TRI_OFF = (0, 512, 896, 1152)
TRI_N = (512, 384, 256, 128)
TRI = 1280
PACKED = ((0, 0, 512), (1, 512, 384), (2, 896, 384))


class Signal:

    def __init__(self, sem):
        self.sem, self.total, self.body = sem, 0, 0


class Point:

    def __init__(self, signal, base, k, loop, rounds_back=0):
        self.counter, self.base, self.k, self.loop, self.rounds_back = signal, base, k, loop, rounds_back

    def back(self, rounds=1):
        return Point(self.counter, self.base, self.k, self.loop, rounds)

    def value(self, loop, i):
        if self.loop is None:
            return self.base + self.k
        per = self.loop.per.get(self.counter, 0)
        if self.loop is loop:
            assert self.base + self.k > 0
            return self.base + self.k + (i * per if per else 0)
        return self.base + self.k + (self.loop.n - 1 - self.rounds_back) * per


class Loop:
    def __init__(self, n):
        self.n, self.per, self.ops = n, {}, {}


class Program:

    def __init__(self, signals, settled):
        self.settled = settled
        self.queues = {e: [] for e in ("sync", "scalar", "vector", "gpsimd", "tensor")}
        self.signals, self.loop = signals, None

    def _queue(self, eng):
        return self.loop.ops.setdefault(eng, []) if self.loop else self.queues[eng]

    def do(self, eng, fn, signal=None, inc=1):
        self._queue(eng).append(("do", fn, signal, inc))
        return self.mark(signal, inc) if signal else None

    def mark(self, signal, inc):
        if self.loop:
            signal.body += inc
        else:
            signal.total += inc
        return self.now(signal)

    def now(self, signal, offset=0):
        return Point(signal, signal.total, signal.body + offset, self.loop)

    def wait(self, eng, *points):
        for p in points:
            if p is not None:
                self._queue(eng).append(("wait", p))

    @contextmanager
    def rounds(self, n):
        loop = self.loop = Loop(n)
        yield
        self.loop = None
        for s in self.signals:
            if s.body:
                loop.per[s] = s.body
                s.total += n * s.body
                s.body = 0
        for eng, ops in loop.ops.items():
            self.queues[eng].append(("loop", loop, ops))

    def run(self, name, eng):
        held = name in ("sync", "scalar", "gpsimd")

        def play(ops, loop, i):
            run = []
            for op in ops:
                if op[0] == "wait":
                    run.append((op[1].counter.sem, op[1].value(loop, i)))
                    continue
                if held and not all(isinstance(v, int) for _, v in run):
                    run = [(s, v if isinstance(v, int) else eng.to_reg(v)) for s, v in run]
                    eng.wait_ge(self.settled.sem, 16)
                for sem, value in run:
                    eng.wait_ge(sem, value)
                run = []
                if op[0] == "do":
                    ins = op[1](eng, i)
                    if op[2]:
                        ins.then_inc(op[2].sem, op[3])
                else:
                    with eng.Fori(0, op[1].n) as j:
                        play(op[2], op[1], j)
            for sem, value in run:
                eng.wait_ge(sem, value)

        play(self.queues[name], None, None)


def one(t, k):
    return t[:, k, :] if isinstance(k, int) else t[:, bass.ds(k, 1), :].squeeze(1)


def span(k, n):
    return slice(k, k + n) if isinstance(k, int) else bass.ds(k, n)


def col(t, k):
    return t[:, span(k, 1)]



VEC_TILES = (
    (("norm_mix_w", 8), ("b_in", 46), ("conv_mix_w", 24), ("b_attn_out", 8), ("norm_ffn_w", 8),
     ("norm_final_w", 8), ("g_ffn1_2", 8), ("g_mix_2", 8), ("g_ffn2_2", 8)),
    (("ffn_conv_w", 3 * FF_TILES), ("ffn_conv_b", FF_TILES), ("g_q_2", 4), ("g_k_2", 4), ("c_2", 8)),
    (("b_mod_2", N_MOD * KC),),
)
VEC = {}
for _t, _tile in enumerate(VEC_TILES):
    _r = _t * P
    for _name, _n in _tile:
        VEC[_name] = _r
        _r += _n
VEC_ROWS = [sum(n for _, n in tile) for tile in VEC_TILES]

LN_EXP = "natural_log_exp_and_others"

C_IDENT, C_ROT, C_DUP, C_TRIU, C_TRIN, C_HEADS, C_LE, C_GT, C_FREQ = 0, 128, 256, 512, 640, 768, 896, 1024, 1152
N_CONST = C_FREQ + 1


def constants():
    c = np.zeros((P, N_CONST), np.float32)
    p, f = np.arange(P)[:, None], np.arange(P)[None, :]
    half = HEAD_DIM // 2
    c[:, C_IDENT:C_IDENT + P] = p == f
    c[:, C_ROT:C_ROT + P] = np.where(f % HEAD_DIM < half, -1.0 * (p == f + half), 1.0 * (p == f - half))
    for kv in range(2):
        c[:, C_DUP + kv * P:C_DUP + (kv + 1) * P] = p == HEAD_DIM * kv + f % HEAD_DIM
    c[:, C_TRIU:C_TRIU + P] = p <= f
    c[:, C_TRIN:C_TRIN + P] = -1.0 * (p >= f)
    c[:, C_HEADS:C_HEADS + P] = p // HEAD_DIM == f // HEAD_DIM
    c[:, C_LE:C_LE + P] = np.where(f <= p, MASKED, 0.0)
    c[:, C_GT:C_GT + P] = np.where(f > p, MASKED, 0.0)
    c[:, C_FREQ] = np.float32(ROPE_THETA) ** (-(2.0 * (np.arange(P) % half)).astype(np.float32) / HEAD_DIM)
    return c


def two_blocks(nc, d, out):
    ctx = ExitStack()
    with ctx:
        def sb(name, shape, dt=F32, stack=ctx):
            return stack.enter_context(nc.sbuf_tensor(name, shape, dt))

        signals = []

        def signal(name):
            s = Signal(ctx.enter_context(nc.semaphore(name)))
            signals.append(s)
            return s

        w_raw = [sb(f"w_raw{n}", [P, KC, P]) for n in range(RAW_SLOTS)]
        w_hi = [sb(f"w_hi{n}", [P, KC, P], F32R) for n in range(CUT_SLOTS)]
        w_lo = [sb(f"w_lo{n}", [P, KC, P], F32R) for n in range(CUT_SLOTS)]
        x = sb("x", [P, KC, SEQ])
        vec = sb("vec", [P, 3 * P])
        consts = sb("consts", [P, N_CONST])
        ident = consts[:, C_IDENT:C_IDENT + P]
        ident_r = sb("ident_r", [P, P], F32R)
        ones = sb("ones", [P, P])
        mask_win = sb("mask_win", [P, 2 * P], F32R)
        mask_first = sb("mask_first", [P, 2 * P], F32R)
        tri_neg = sb("tri_neg", [P, P], F32R)
        ones_neg = sb("ones_neg", [P, P], F32R)
        ones_r = sb("ones_r", [P, P], F32R)
        small = sb("small", [P, 40])
        sink_c = sb("sink_c", [P, N_SWA_HEADS])
        bf_c = sb("bf_c", [P, N_FOX])
        mod = sb("mod", [P, N_MOD * KC])
        gains = sb("gains", [P, 6 * KC])
        c_act = sb("c_act", [P, KC])
        ssum = sb("ssum", [P, SEQ])
        rstd = sb("rstd", [P, SEQ])
        t_a = [sb(f"t_a{n}", [P, SEQ + 2]) for n in range(2)]
        t_b = [sb(f"t_b{n}", [P, SEQ]) for n in range(2)]
        f_col = sb("f_col", [P, TB, N_FOX])

        u_hi = sb("u_hi", [P, KC, SEQ], F32R)
        u_lo = sb("u_lo", [P, KC, SEQ], F32R)
        with ExitStack() as r1:
            fq, fk, fv, sv = (sb(n, [P, KC // 2, SEQ], F32, r1) for n in ("fq", "fk", "fv", "sv"))
        with ExitStack() as r1:
            y_hi = sb("y_hi", [P, KC, SEQ], F32R, r1)
            y_lo = sb("y_lo", [P, KC, SEQ], F32R, r1)
            ctx.push(r1.pop_all())
        with ExitStack() as r2:
            x_in = sb("x_in", [P, TB, D_MODEL], F32, r2)
            vec_rows = sb("vec_rows", [P, 3, P], F32, r2)
        with ExitStack() as r2:
            mod_raw_v = [sb(f"mod_raw_v{n}", [P, KC, P], F32, r2) for n in range(2)]
            mod_raw = [sb(f"mod_raw{n}", [P, KC, P], F32, r2) for n in range(2)]
        with ExitStack() as r2:
            sq, sk = (sb(n, [P, KC // 2, SEQ], F32, r2) for n in ("sq", "sk"))
            nf_hi = sb("nf_hi", [N_FOX, SEQ], F32R, r2)
            nf_lo = sb("nf_lo", [N_FOX, SEQ], F32R, r2)
            f_hi = sb("f_hi", [P, 2, SEQ], F32R, r2)
            f_lo = sb("f_lo", [P, 2, SEQ], F32R, r2)
        with ExitStack() as r2:
            g_conv = sb("g_conv", [P, KC, SEQ], F32, r2)
            q1 = sb("q1", [P, KC // 2, SEQ], F32, r2)
            k1 = sb("k1", [P, 2, SEQ], F32, r2)
            v1 = sb("v1", [P, TB, P], F32, r2)
            ctx.push(r2.pop_all())
        with ExitStack() as r3:
            mod_acc = sb("mod_acc", [P, N_MOD * KC, P], F32, r3)
        with ExitStack() as r3:
            o_hi = sb("o_hi", [P, KC // 2, SEQ], F32R, r3)
            o_lo = sb("o_lo", [P, KC // 2, SEQ], F32R, r3)
        with ExitStack() as r3:
            q_hi = sb("q_hi", [P, 2, SEQ], F32R, r3)
            q_lo = sb("q_lo", [P, 2, SEQ], F32R, r3)
            v_hi = sb("v_hi", [P, TB, 2, P], F32R, r3)
            v_lo = sb("v_lo", [P, TB, 2, P], F32R, r3)
            k_hi = sb("k_hi", [P, SEQ], F32R, r3)
            k_lo = sb("k_lo", [P, SEQ], F32R, r3)
            att_a = sb("att_a", [P, TRI], F32, r3)
            att_b = sb("att_b", [P, TRI], F32, r3)
            p_hi = sb("p_hi", [P, TRI], F32R, r3)
            p_lo = sb("p_lo", [P, TRI], F32R, r3)
            ctx.push(r3.pop_all())
        ps = ctx.enter_context(nc.psum_tensor("ps", [P, 8, SEQ], F32))
        AUX = 7

        act = signal("act_done")
        dve = signal("dve_done")
        pool = signal("pool_done")
        pe = signal("pe_done")
        raw_in = [signal(f"raw_in{n}") for n in range(RAW_SLOTS)]
        hi_cut = signal("hi_cut")
        lo_cut = signal("lo_cut")
        unit_done = signal("unit_done")
        bank_free = [signal(f"bank_free{n}") for n in range(2)]
        x_landed, const_landed, vec_landed = signal("x_landed"), signal("const_landed"), signal("vec_landed")
        pos_landed, row_landed = signal("pos_landed"), signal("row_landed")
        mod_in = [signal(f"mod_in{n}") for n in range(2)]
        mod_in_v = [signal(f"mod_in_v{n}") for n in range(2)]
        mod_taken_v = [signal(f"mod_taken_v{n}") for n in range(2)]
        out_written = signal("out_written")

        pr = Program(signals, const_landed)
        do, wait, now = pr.do, pr.wait, pr.now
        S, A, V, G, T = "sync", "scalar", "vector", "gpsimd", "tensor"

        def a_fn(out_, in_, func, bias=0.0, scale=1.0, accum=None, sig=act):
            def fn(e, i):
                o, n, b, s, ac = (f(i) if callable(f) else f for f in (out_, in_, bias, scale, accum))
                kw = {"accum_out": ac} if ac is not None else {}
                return e.activation(o, n, func, bias=b, scale=s, **kw)
            return do(A, fn, sig)

        def v_tt(out_, a, b, op, sig=dve, eng=V):
            def fn(e, i):
                o, p_, q_ = (f(i) if callable(f) else f for f in (out_, a, b))
                return e.tensor_tensor(o, p_, q_, op)
            return do(eng, fn, sig)

        def v_ts(out_, a, s1, op0, s2=None, op1=None, sig=dve, eng=V):
            def fn(e, i):
                o, p_, c1, c2 = (f(i) if callable(f) else f for f in (out_, a, s1, s2))
                return e.tensor_scalar(o, p_, c1, c2, op0, op1) if op1 is not None else e.tensor_scalar(o, p_, c1, None, op0)
            return do(eng, fn, sig)

        def v_stt(out_, a, s, b, op0, op1, sig=dve):
            def fn(e, i):
                o, p_, c, q_ = (f(i) if callable(f) else f for f in (out_, a, s, b))
                return e.scalar_tensor_tensor(out=o, in0=p_, scalar=c, in1=q_, op0=op0, op1=op1)
            return do(V, fn, sig)

        def copy(eng, out_, in_, sig):
            def fn(e, i):
                o, n = (f(i) if callable(f) else f for f in (out_, in_))
                return e.activation(o, n, ACT.Copy) if eng == A else e.tensor_copy(o, n)
            return do(eng, fn, sig)

        def memset(eng, t, v, sig):
            return do(eng, lambda e, i: e.memset(t, v), sig)

        def dma(eng, dst, src, sig):
            def fn(e, i):
                return e.dma_start(dst(i) if callable(dst) else dst, src(i) if callable(src) else src)
            return do(eng, fn, sig, 16)

        def mm(out_, lhsT, rhs, start, stop=True, sig=None, skip=False):
            return do(T, lambda e, i: e.matmul(out_, lhsT, rhs, start=start, stop=stop, skip_group_check=skip), sig)

        def transpose(out_, in_, n, sig=None):
            return do(T, lambda e, i: e.transpose(out_, in_, consts[0:n, C_IDENT:C_IDENT + n]), sig)

        def three(out_, left, right, start, stop, sig=None, skip=False):
            mm(out_, left[0], right[0], start, skip, skip=skip and not start)
            mm(out_, left[0], right[1], False, skip, skip=skip)
            return mm(out_, left[1], right[0], False, stop or skip, sig, skip=skip)

        def vcol(name, k=0):
            return lambda i: col(vec, VEC[name] + (k(i) if callable(k) else k))

        def f32(t):
            return t.bitcast(F32)

        ring = {"u": 0, "lead": CUT_SLOTS}

        def strip(w, column, k0=0, n_k=KC):
            v = w.rearrange("(k p) n -> p k n", p=P)

            def at(i):
                c = column(i) if callable(column) else column
                return v[:, k0:k0 + n_k, c:c + P] if isinstance(c, int) else v[:, k0:k0 + n_k, bass.ds(c, P)]
            return at

        def cut(v):
            slot, c = v % RAW_SLOTS, v % CUT_SLOTS
            wait(A, now(raw_in[slot], 16))
            if v >= CUT_SLOTS:
                wait(A, now(unit_done))
            copy(A, w_hi[c][:, :, :], w_raw[slot][:, :, :], hi_cut)
            wait(V, now(hi_cut))
            v_tt(w_lo[c][:, :, :], w_raw[slot][:, :, :], f32(w_hi[c][:, :, :]), ALU.subtract, lo_cut)

        def unit(src, acts, n_k=KC, k0=0, ready=None, ahead=True, bank=None, part=None):
            u = ring["u"]
            slot, c = u % RAW_SLOTS, u % CUT_SLOTS
            b = u % 2 if bank is None else bank
            if u >= RAW_SLOTS:
                wait(S, now(lo_cut, 1 - RAW_SLOTS - ring["lead"]))
            dma(S, w_raw[slot][:, 0:n_k, :], src, raw_in[slot])
            wait(T, now(lo_cut, 1 - ring["lead"]))
            if u >= 2:
                wait(T, now(bank_free[u % 2]))
            ready = ready or {}
            last = None
            for k in range(n_k):
                wait(T, ready.get(k))
                last = three(ps[:, b, :], (w_hi[c][:, k, :], w_lo[c][:, k, :]),
                             (acts[0][:, k0 + k, :], acts[1][:, k0 + k, :]), k == 0 and part != 1,
                             k == n_k - 1 and part != 0, unit_done if k == n_k - 1 else None)
            ring["u"] += 1
            if ahead:
                cut(u + 2)
            else:
                ring["lead"] -= 1
            return b, last

        def rounds(n):
            @contextmanager
            def loop():
                u0 = ring["u"]
                with pr.rounds(n):
                    yield
                body = ring["u"] - u0
                assert body % RAW_SLOTS == 0
                ring["u"] += (n - 1) * body
            return loop()

        def bank(b):
            return ps[:, b, :]

        dma(S, consts[:, :], d["consts"], const_landed)
        x_tok = d["x"][0].rearrange("(t p) n -> p t n", p=P)
        for tb in range(TB):
            dma(S, x_in[:, tb, :], x_tok[:, tb, :], x_landed)
        for t, tile in enumerate(VEC_TILES):
            for name, n in tile:
                r = VEC[name] - t * P
                src = d[name]
                flat = src.rearrange(" ".join("abcd"[:len(src.shape)]) + " -> (" + " ".join("abcd"[:len(src.shape)]) + ")") \
                    if len(src.shape) > 1 else src
                dma(A, vec_rows[r:r + n, t, :], flat.rearrange("(r p) -> r p", p=P), vec_landed)
        pos32 = t_a[0][:, 2:2 + SEQ]
        dma(A, pos32.bitcast(I32), d["positions"].broadcast_to([P, SEQ]), pos_landed)
        dma(A, sink_c[:, :], d["sinks"].broadcast_to([P, N_SWA_HEADS]), row_landed)
        dma(A, bf_c[:, :], d["b_f_2"].broadcast_to([P, N_FOX]), row_landed)

        memset(G, ones[:, :], 1.0, pool)
        ones_set = memset(G, t_a[0][:, 0:2], 0.0, pool)
        memset(G, t_a[1][:, 0:2], 0.0, pool)
        for t in (q_hi, q_lo, v_hi, v_lo):
            zeros_set = memset(G, f32(t[:]), 0.0, pool)

        wait(V, now(const_landed))
        wait(V, ones_set)
        copy(V, ident_r[:, :], ident, dve)
        copy(V, mask_win[:, 0:P], consts[:, C_LE:C_LE + P], dve)
        copy(V, mask_win[:, P:2 * P], consts[:, C_GT:C_GT + P], dve)
        v_ts(mask_first[:, 0:P], ones[:, :], MASKED, ALU.mult)
        copy(V, mask_first[:, P:2 * P], consts[:, C_GT:C_GT + P], dve)
        copy(V, tri_neg[:, :], consts[:, C_TRIN:C_TRIN + P], dve)
        v_ts(ones_neg[:, :], ones[:, :], -1.0, ALU.mult)
        copy(V, ones_r[:, :], ones[:, :], dve)
        memset(V, ssum[:, :], 0.0, dve)

        wait(T, now(const_landed))
        wait(T, now(x_landed))
        x_ready = []
        for c in range(KC):
            b = 2 + c % 4
            if c >= 4:
                wait(T, x_ready[c - 4])
            for tb in range(TB):
                t = transpose(ps[:, b, tb * P:(tb + 1) * P], x_in[:, tb, c * P:(c + 1) * P], P, pe if tb == TB - 1 else None)
            wait(A, t)
            x_ready.append(copy(A, x[:, c, :], bank(b), act))

        def add_square(c, s, x_done, first=False):
            wait(A, x_done)
            wait(A, now(dve))
            sq_done = a_fn(t_b[s][:, :], lambda i: one(x, c(i) if callable(c) else c), ACT.Square)
            wait(V, sq_done)
            wait(V, now(dve))
            if first:
                return copy(V, ssum[:, :], t_b[s][:, :], dve)
            return v_tt(ssum[:, :], ssum[:, :], t_b[s][:, :], ALU.add)

        ssum_cleared = now(dve)

        def sum_squares(chunk):
            squared, added = [], []
            for c in range(KC + 1):
                if c < KC:
                    wait(A, chunk(c))
                    if c >= 2:
                        wait(A, added[c - 2])
                    squared.append(a_fn(t_b[c % 2][:, :], x[:, c, :], ACT.Square))
                if c >= 1:
                    wait(V, squared[c - 1])
                    if c == 1:
                        wait(V, ssum_cleared)
                        added.append(copy(V, ssum[:, :], t_b[0][:, :], dve))
                    else:
                        wait(V, added[-1])
                        added.append(v_tt(ssum[:, :], ssum[:, :], t_b[(c - 1) % 2][:, :], ALU.add))
            return added[-1]

        wait(T, now(vec_landed))
        for t, rows in enumerate(VEC_ROWS):
            tr = transpose(ps[:, 6, t * P:t * P + rows], vec_rows[0:rows, t, :], rows, pe)
        wait(V, tr)
        for t, rows in enumerate(VEC_ROWS):
            vec_done = copy(V, vec[:, t * P:t * P + rows], ps[:, 6, t * P:t * P + rows], dve)
        ssum_done = sum_squares(lambda c: x_ready[c])
        wait(A, vec_done)
        silu_c = a_fn(c_act[:, :], vec[:, VEC["c_2"]:VEC["c_2"] + KC], ACT.Silu)

        def root(bank_, eps, sig_ready, n):
            do(A, lambda e, i: e.preload_act_table_set(LN_EXP))
            wait(A, sig_ready)
            wait(A, now(dve))
            r = a_fn(rstd[:, :], bank(bank_), ACT.Ln, bias=eps_col(eps), scale=1.0 / n)
            wait(A, r)
            return a_fn(rstd[:, :], rstd[:, :], ACT.Exp, scale=-0.5)

        eps_at = {EPS1: 0, EPS2: 1}
        memset(G, small[:, 0:1], EPS1, pool)
        eps_set = memset(G, small[:, 1:2], EPS2, pool)
        wait(A, eps_set)

        def eps_col(eps):
            return small[:, eps_at[eps]:eps_at[eps] + 1]

        def norm(gain, shift, eps, sums_done, beside=lambda: None):
            wait(T, sums_done)
            total = mm(bank(AUX), ones[:, :], ssum[:, :], True, True, pe)
            beside()
            rstd_done = root(AUX, eps, total, D_MODEL)
            if ring["u"]:
                wait(A, now(unit_done))
            ready = {}
            pending = []

            def low(c, hi):
                wait(V, hi)
                if shift is None:
                    ready[c] = v_tt(u_lo[:, c, :], t_b[c % 2][:, :], f32(u_hi[:, c, :]), ALU.subtract)
                else:
                    ready[c] = v_stt(u_lo[:, c, :], t_b[c % 2][:, :], shift(c), f32(u_hi[:, c, :]), ALU.add, ALU.subtract)

            wait(V, rstd_done)
            for c in range(KC):
                if len(pending) == 2:
                    low(*pending.pop(0))
                    wait(V, ready[c - 2])
                t = v_stt(t_b[c % 2][:, :], x[:, c, :], gain(c), rstd[:, :], ALU.mult, ALU.mult)
                wait(A, t)
                hi = a_fn(u_hi[:, c, :], t_b[c % 2][:, :], ACT.Identity, bias=shift(c) if shift else 0.0)
                pending.append((c, hi))
            for args in pending:
                low(*args)
            return ready

        for v in range(CUT_SLOTS):
            cut(v)
        ready = norm(lambda c: vcol("norm_mix_w", c), None, EPS1, ssum_done)
        u_act = (u_hi, u_lo)
        w1 = d["w_in"][0]

        def b_in(section, tile=0):
            base = IN1[section] // P
            return vcol("b_in", (lambda i: base + tile(i)) if callable(tile) else base + tile)

        ang, rnd, cos_t, sin_t = att_a[:, 0:SEQ], att_a[:, SEQ:2 * SEQ], att_b[:, 0:SEQ], att_b[:, SEQ:2 * SEQ]
        wait(V, now(pos_landed))
        p0 = copy(V, ang, pos32.bitcast(I32), dve)
        wait(V, p0)
        p0 = v_ts(ang, ang, consts[:, C_FREQ:C_FREQ + 1], ALU.mult)
        for table, turn, add in ((sin_t, 0.0, 0.0), (cos_t, 0.25, TWO_PI / 4)):
            wait(V, now(dve))
            v_ts(rnd, ang, 1.0 / TWO_PI, ALU.mult, turn, ALU.add)
            wait(V, now(dve))
            v_ts(rnd, rnd, ROUND, ALU.add)
            wait(V, now(dve))
            v_ts(rnd, rnd, ROUND, ALU.subtract)
            wait(V, now(dve))
            v_stt(table, rnd, -PI_A, ang, ALU.mult, ALU.add)
            wait(V, now(dve))
            v_stt(table, rnd, -PI_B, table, ALU.mult, ALU.add)
            wait(V, now(dve))
            if add:
                v_ts(table, table, add, ALU.add)
                wait(V, now(dve))
            t = v_ts(table, table, 3.141592, ALU.min, -3.141592, ALU.max)
            wait(A, t)
            tables_done = a_fn(table, table, ACT.Sin)

        x_in_free = now(pe)
        wait(A, x_in_free)

        def rope(dst, raw_done, c):
            wait(T, raw_done)
            wait(T, now(dve))
            r = mm(bank(4 + c % 2), consts[:, C_ROT:C_ROT + P], dst, True, True, pe)
            wait(V, r)
            wait(V, tables_done)
            s = v_tt(t_b[0][:, :], bank(4 + c % 2), sin_t, ALU.mult)
            t = v_tt(t_b[1][:, :], dst, cos_t, ALU.mult)
            wait(V, t)
            r = v_tt(dst, t_b[0][:, :], t_b[1][:, :], ALU.add)
            wait(V, r)
            return r

        raws = []
        for c in range(5):
            b, done = unit(strip(w1, IN1["q"] + c * P), u_act, ready=ready if c == 0 else None)
            dst = q1[:, c, :] if c < 4 else k1[:, 0, :]
            wait(A, done)
            raws.append((dst, a_fn(dst, bank(b), ACT.Identity, bias=b_in("q", c), sig=bank_free[b])))
            if c:
                rope(*raws[c - 1], c - 1)
        b, done = unit(strip(w1, IN1["v"]), u_act)
        k_roped = rope(*raws[4], 4)
        v_t = t_a[0][:, 2:2 + SEQ]
        wait(A, done)
        t = a_fn(v_t, bank(b), ACT.Identity, bias=b_in("v", 0), sig=bank_free[b])
        wait(T, t)
        for tb in range(TB):
            t = transpose(ps[:, 6, tb * P:(tb + 1) * P], v_t[:, tb * P:(tb + 1) * P], P, pe)
        wait(A, t)
        v_done = copy(A, v1[:, :, :], bank(6).rearrange("p (t n) -> p t n", n=P), act)
        wait(T, k_roped)
        for kv in range(2):
            t = mm(bank(2 + kv), consts[:, C_DUP + kv * P:C_DUP + (kv + 1) * P], k1[:, 0, :], True, True, pe)
        wait(A, t)
        copy(A, k1[:, 0, :], bank(2), act)
        k_done = copy(A, k1[:, 1, :], bank(3), act)

        SCALE = HEAD_DIM ** -0.5

        def stage_q_k(q_src, k_src):
            for n in range(2):
                rows = slice(HEAD_DIM * n, HEAD_DIM * (n + 1))
                a_fn(q_hi[rows, n, :], lambda i, r=rows: q_src(i)[r, :], ACT.Copy, scale=SCALE)
                wait(V, now(act))
                v_stt(q_lo[rows, n, :], lambda i, r=rows: q_src(i)[r, :], SCALE, f32(q_hi[rows, n, :]), ALU.mult, ALU.subtract)
            kh = copy(A, k_hi[:, :], k_src, act)
            wait(V, kh)
            return v_tt(k_lo[:, :], k_src, f32(k_hi[:, :]), ALU.subtract)

        def stage_v(v_src):
            for n in range(2):
                cols = slice(HEAD_DIM * n, HEAD_DIM * (n + 1))
                vh = copy(A, v_hi[:, :, n, cols], lambda i, n=n: v_src(i, n), act)
                wait(V, vh)
                v_cut = v_tt(v_lo[:, :, n, cols], lambda i, n=n: v_src(i, n), f32(v_hi[:, :, n, cols]), ALU.subtract)
            return v_cut

        def stage(q_src, k_src, v_src, sources):
            wait(A, *sources)
            wait(V, *sources)
            wait(A, now(pe))
            wait(A, zeros_set)
            return stage_q_k(q_src, k_src), stage_v(v_src)

        W_BANK = (2, 3)
        W_N = 2 * P
        O_BANK = AUX

        def win_scores(n, k_cut):
            wait(T, k_cut)
            for b in range(TB):
                reg = ps[:, W_BANK[b // 2], (b % 2) * W_N:(b % 2 + 1) * W_N]
                ks = slice(max(b - 1, 0) * P, (b + 1) * P)
                mm(reg, ident_r[:, :], (mask_win if b else mask_first)[:, :], True, False)
                own = reg if b else reg[:, P:W_N]
                bs = slice(b * P, (b + 1) * P)
                s = three(own, (q_hi[:, n, bs], q_lo[:, n, bs]), (k_hi[:, ks], k_lo[:, ks]), False, True,
                          pe if b == TB - 1 else None)
            return s

        def win_softmax(n, head, scores):
            mx, nm, den, es = small[:, 4:8], small[:, 8:12], small[:, 12:16], small[:, 16:20]
            sink = lambda i: col(sink_c, head(i))
            s4 = ps[:, W_BANK[0]:W_BANK[1] + 1, :].rearrange("p b (h n) -> p (b h) n", n=W_N)
            wait(V, scores)
            m1 = do(V, lambda e, i: e.tensor_reduce(mx, s4, AX_X, ALU.max), dve)
            wait(V, m1)
            m2 = v_ts(nm, mx, sink, ALU.max, -1.0, ALU.mult)
            wait(A, m2)
            for b in range(TB):
                reg = ps[:, W_BANK[b // 2], (b % 2) * W_N:(b % 2 + 1) * W_N]
                a_fn(att_a[:, b * W_N:(b + 1) * W_N], reg, ACT.Exp, bias=nm[:, b:b + 1], accum=den[:, b:b + 1])
            ex = a_fn(es, nm, ACT.Exp, bias=sink)
            wait(V, ex)
            v_tt(den, den, es, ALU.add)
            wait(V, now(dve))
            do(V, lambda e, i: e.reciprocal(den, den), dve)
            wait(V, now(dve))
            for b in range(TB):
                w = att_a[:, b * W_N:(b + 1) * W_N]
                r = v_ts(w, w, den[:, b:b + 1], ALU.mult)
            return r

        def win_transpose(probs):
            wait(T, probs)
            for j in range(TB):
                for b in range(j, min(j + 2, TB)):
                    src = att_a[:, b * W_N + (0 if b > j else P):b * W_N + (P if b > j else W_N)]
                    at = (j % 2) * W_N + (b - j) * P
                    t = transpose(ps[:, 4 + j // 2, at:at + P], src, P, pe)
            return t

        def cut_from_banks(pieces, transposed):
            wait(A, transposed)
            cuts = []
            for b, at, n in pieces:
                h = copy(A, p_hi[:, at:at + n], ps[:, b, 0:n], act)
                wait(V, h)
                cuts.append(v_tt(p_lo[:, at:at + n], ps[:, b, 0:n], f32(p_hi[:, at:at + n]), ALU.subtract))
            return cuts

        def win_values(n, p_cut, v_cut):
            wait(T, p_cut[-1])
            wait(T, v_cut)
            for j in range(TB):
                w = min(2, TB - j) * P
                at = j * W_N
                o = three(ps[:, O_BANK, j * P:j * P + w], (v_hi[:, j, n, :], v_lo[:, j, n, :]),
                          (p_hi[:, at:at + w], p_lo[:, at:at + w]), n == 0 and j == 0, True,
                          pe if j == TB - 1 else None, skip=True)
            return o

        w_sources = (now(row_landed), now(dve), now(act), now(bank_free[1]), now(bank_free[0]), k_done, v_done)
        TAP = KC

        def conv(dst, src, w_col, bias=None):
            v_ts(dst, src[:, 2:2 + SEQ], w_col(2), ALU.mult, *(() if bias is None else (bias, ALU.add)))
            wait(V, now(dve))
            v_stt(dst, src[:, 1:1 + SEQ], w_col(1), dst, ALU.mult, ALU.add)
            wait(V, now(dve))
            return v_stt(dst, src[:, 0:SEQ], w_col(0), dst, ALU.mult, ALU.add)

        with rounds(4):
            st, y_cuts = {}, [None, None]
            last_round = now(dve)
            for j in range(2):
                tile = lambda i, j=j: i * 2 + j
                for s, sec in enumerate(("cc", "cx", "cb", "gc")):
                    step = 4 * j + s
                    if step == 0:
                        st["k"], st["v"] = stage(
                            lambda i: one(q1, i), lambda i: one(k1, i // 2),
                            lambda i, n: v1[:, :, bass.ds((i // 2) * HEAD_DIM, HEAD_DIM)], w_sources)
                    if step == 1:
                        st["s"] = win_scores(0, st["k"])
                        st["p"] = win_softmax(0, lambda i: i * 2, st["s"])
                    if step == 2:
                        t = win_transpose(st["p"])
                        st["c"] = cut_from_banks(((4, 0, 512), (5, 512, 384)), t)
                    if step == 3:
                        win_values(0, st["c"], st["v"])
                        st["s"] = win_scores(1, st["k"])
                        st["p"] = win_softmax(1, lambda i: i * 2 + 1, st["s"])
                    if step == 4:
                        t = win_transpose(st["p"])
                        st["c"] = cut_from_banks(((4, 0, 512), (5, 512, 384)), t)
                    if step == 5:
                        o = win_values(1, st["c"], st["v"])
                        wait(A, o)
                        copy(A, lambda i: one(q1, i), bank(O_BANK), act)
                    b, done = unit(strip(w1, lambda i, sec=sec, j=j: i * (2 * P) + (IN1[sec] + j * P)), u_act)
                    y = t_b[j]
                    if sec == "cc":
                        wait(A, done)
                        wait(A, last_round)
                        cc = a_fn(y[:, :], bank(b), ACT.Identity, bias=b_in("cc", tile), sig=bank_free[b])
                    elif sec == "cx":
                        wait(V, done)
                        wait(V, cc)
                        wait(V, now(dve))
                        cx = v_stt(t_a[j][:, 2:2 + SEQ], bank(b), b_in("cx", tile), y[:, :], ALU.add, ALU.mult, bank_free[b])
                        wait(V, cx)
                        cv = conv(y[:, :], t_a[j], lambda tap, t=tile: vcol("conv_mix_w", lambda i: tap * TAP + t(i)))
                    elif sec == "cb":
                        wait(V, done)
                        wait(V, cv)
                        yb = v_stt(y[:, :], bank(b), b_in("cb", tile), y[:, :], ALU.add, ALU.mult, bank_free[b])
                        wait(A, yb)
                        h = copy(A, lambda i, t=tile: one(y_hi, t(i)), y[:, :], act)
                        wait(V, h)
                        y_cuts[j] = v_tt(lambda i, t=tile: one(y_lo, t(i)), y[:, :], lambda i, t=tile: f32(one(y_hi, t(i))), ALU.subtract)
                    else:
                        wait(A, done)
                        g_done = a_fn(lambda i, t=tile: one(g_conv, t(i)), bank(b), ACT.Sigmoid, bias=b_in("gc", tile), sig=bank_free[b])

        for c in range(KC // 2):
            if c == 0:
                wait(A, now(pe))
            wait(A, now(act))
            h = copy(A, o_hi[:, c, :], q1[:, c, :], act)
            wait(V, h)
            o_cut = v_tt(o_lo[:, c, :], q1[:, c, :], f32(o_hi[:, c, :]), ALU.subtract)
        y_act = (y_hi, y_lo)

        def chunks_ready(cuts, n):
            return {n - 2: cuts[0], n - 1: cuts[1]} | ({0: cuts[1].back()} if n > 2 else {})


        with rounds(2):
            for c in range(4):
                tile = lambda i, c=c: i * 4 + c
                b, done = unit(strip(d["w_conv_out"][0], lambda i, c=c: i * (4 * P) + c * P), y_act,
                               ready=chunks_ready(y_cuts, KC) if c == 0 else None)
                wait(V, done)
                wait(V, g_done)
                g = lambda i, t=tile: one(g_conv, t(i))
                skipped = v_tt(g, g, bank(b), ALU.mult, bank_free[b])

        m_cuts = [None, None]
        with rounds(4):
            for j in range(2):
                tile = lambda i, j=j: i * 2 + j
                b, done = unit(strip(w1, lambda i, j=j: i * (2 * P) + (IN1["ga"] + j * P)), u_act)
                wait(A, done)
                wait(A, now(dve))
                ga = a_fn(t_b[j][:, :], bank(b), ACT.Sigmoid, bias=b_in("ga", tile), sig=bank_free[b])
                if j == 0:
                    wait(T, o_cut)
                b, done = unit(strip(d["w_attn_out"][0], lambda i, j=j: i * (2 * P) + j * P, n_k=KC // 2), (o_hi, o_lo), n_k=KC // 2)
                wait(V, done)
                wait(V, ga)
                wait(V, now(dve))
                t = v_stt(t_a[j][:, 2:2 + SEQ], bank(b), vcol("b_attn_out", tile), t_b[j][:, :], ALU.add, ALU.mult, bank_free[b])
                wait(V, t)
                wait(V, skipped)
                t = v_tt(t_b[j][:, :], t_a[j][:, 2:2 + SEQ], lambda i, t=tile: one(g_conv, t(i)), ALU.add)
                wait(A, t)
                h = copy(A, lambda i, t=tile: one(y_hi, t(i)), t_b[j][:, :], act)
                wait(V, h)
                m_cuts[j] = v_tt(lambda i, t=tile: one(y_lo, t(i)), t_b[j][:, :], lambda i, t=tile: f32(one(y_hi, t(i))), ALU.subtract)

        w_mod = d["w_mod_2"][0].rearrange("(k p) n -> p k n", p=P)
        wait(G, silu_c)
        wait(V, silu_c)
        wait(G, m_cuts[1])
        wait(G, now(unit_done))
        MOD_TILES = N_MOD * KC
        MOD_POOL = MOD_TILES - sum(FF_PARTS[:-1])
        for n in range(2):
            memset(G, mod_raw_v[n][:, 0, 0:1], 0.0, mod_taken_v[n])

        def mod_products(eng, sig, r, landed):
            wait(eng, landed)
            v_tt(r[:, :, :], r[:, :, :], c_act[:, :].unsqueeze(2).broadcast_to([P, KC, P]), ALU.mult, sig, eng)

        def mod_sums(eng, sig, r, dst):
            for h in (4, 2):
                wait(eng, now(sig))
                v_tt(r[:, 0:h, :], r[:, 0:h, :], r[:, h:2 * h, :], ALU.add, sig, eng)
            wait(eng, now(sig))
            return v_tt(dst, r[:, 0, :], r[:, 1, :], ALU.add, mod_taken_v[mod_raw_v.index(r)] if eng == V else sig, eng)

        def mod_strip(tile):
            return lambda i: w_mod[:, :, bass.ds(tile(i) * P, P)]

        def mod_step(half, j, tile):
            if half == 0:
                wait(A, now(mod_taken_v[j]))
                dma(A, mod_raw_v[j][:, :, :], mod_strip(lambda i: tile(i) + MOD_POOL), mod_in_v[j])
            else:
                mod_products(V, dve, mod_raw_v[j], now(mod_in_v[j]))
                mod_sums(V, dve, mod_raw_v[j], lambda i: one(mod_acc, tile(i) + MOD_POOL))

        def mod_tiles(more):
            for n in range(2):
                mod_products(G, pool, mod_raw[n], now(mod_in[n]))
                s = mod_sums(G, pool, mod_raw[n], lambda i, n=n: one(mod_acc, i * 2 + n if more else MOD_POOL - 2 + n))
                if more:
                    wait(G, s)
                    dma(G, mod_raw[n][:, :, :], mod_strip(lambda i, n=n: i * 2 + (n + 2)), mod_in[n])

        for n in range(2):
            dma(G, mod_raw[n][:, :, :], w_mod[:, :, n * P:(n + 1) * P], mod_in[n])
        with pr.rounds(MOD_POOL // 2 - 1):
            mod_tiles(True)
        mod_tiles(False)
        mod_summed = now(pool)

        def residual(w, acts, ready, gain=None, n_k=KC, k_row=0, squares=False, after=None):
            def four(tiles, static):
                for c, tile in enumerate(tiles):
                    b, done = unit(strip(w, lambda i, t=tile: t(i) * P, k_row, n_k), acts, n_k=n_k,
                                   ready=ready if tile is tiles[0] and (not static or tile(0) == 0) else None,
                                   ahead=not static or tile(0) < KC - 2)
                    if after and tile(0):
                        after(tile(0) - 1, r)
                    wait(V, done)
                    xt = lambda i, t=tile: one(x, t(i))
                    if gain is None:
                        r = v_tt(xt, xt, bank(b), ALU.add, bank_free[b])
                    else:
                        r = v_stt(xt, bank(b), lambda i, t=tile: gain(t(i)), xt, ALU.mult, ALU.add, bank_free[b])
                    if squares:
                        r = add_square(tile, c % 2, r)
                if after:
                    after(KC - 1, r)
                return r

            if after:
                return four([lambda i, c=c: c for c in range(KC)], True)
            with rounds(2):
                r = four([lambda i, c=c: i * 4 + c for c in range(4)], False)
            return r

        def clear_ssum():
            wait(V, now(pe))
            memset(V, ssum[:, :], 0.0, dve)

        clear_ssum()
        sums = residual(d["w_mix_out"][0], y_act, chunks_ready(m_cuts, KC), squares=True)

        def ffn(ready, strips, hidden, w_down, gain, after=None, beside=None):
            t0 = 0
            for n, tiles in enumerate(FF_PARTS):
                h_cut = [None, None]
                with rounds(tiles // 2):
                    for j in range(2):
                        first = None
                        for s in range(2):
                            w, c0 = strips[s]
                            b, done = unit(strip(w, lambda i, j=j, c0=c0, t0=t0: i * (2 * P) + (c0 + (t0 + j) * P)), u_act,
                                           ready=ready if n == 0 and j == 0 and s == 0 else None)
                            first = hidden(s, b, done, j, lambda i, j=j, t0=t0: i * 2 + (t0 + j), first)
                            if beside and s == 0 and n < len(FF_PARTS) - 1:
                                beside(0, j, lambda i, j=j, t0=t0: i * 2 + (t0 + j))
                        wait(A, first)
                        h = copy(A, lambda i, j=j: one(y_hi, i * 2 + j), t_b[j][:, :], act)
                        wait(V, h)
                        h_cut[j] = v_tt(lambda i, j=j: one(y_lo, i * 2 + j), t_b[j][:, :],
                                        lambda i, j=j: f32(one(y_hi, i * 2 + j)), ALU.subtract)
                        if beside and n < len(FF_PARTS) - 1:
                            beside(1, j, lambda i, j=j, t0=t0: i * 2 + (t0 + j))
                last = n == len(FF_PARTS) - 1
                if last:
                    clear_ssum()
                r = residual(w_down, y_act, chunks_ready(h_cut, tiles), gain, tiles, t0,
                             squares=last and not after, after=after if last else None)
                t0 += tiles
            return r

        def conv_hidden(s, b, done, j, tile, before):
            if s == 0:
                wait(A, done)
                wait(A, now(dve))
                t = a_fn(t_a[j][:, 2:2 + SEQ], bank(b), ACT.Copy, sig=bank_free[b])
                wait(V, t)
                wait(V, now(act))
                cv = conv(t_b[j][:, :], t_a[j], lambda tap: vcol("ffn_conv_w", lambda i: tap * FF_TILES + tile(i)),
                          vcol("ffn_conv_b", tile))
                wait(A, cv)
                return a_fn(t_b[j][:, :], t_b[j][:, :], ACT.Silu)
            wait(V, done)
            wait(V, before)
            return v_tt(t_b[j][:, :], t_b[j][:, :], bank(b), ALU.mult, bank_free[b])

        def glu_hidden(s, b, done, j, tile, before):
            if s == 0:
                wait(A, done)
                wait(A, now(dve))
                return a_fn(t_b[j][:, :], bank(b), ACT.Silu, sig=bank_free[b])
            wait(V, done)
            wait(V, before)
            return v_tt(t_b[j][:, :], t_b[j][:, :], bank(b), ALU.mult, bank_free[b])

        ready = norm(lambda c: vcol("norm_ffn_w", c), None, EPS1, sums)
        up1 = d["w_ffn_up"][0]
        sums = ffn(ready, ((up1, 0), (up1, D_FF)), conv_hidden, d["w_ffn_down"][0], None, beside=mod_step)
        mod_v_summed = [now(s) for s in mod_taken_v]

        wait(T, sums)
        total = mm(bank(AUX), ones[:, :], ssum[:, :], True, True, pe)
        wait(T, mod_summed)
        wait(T, *mod_v_summed)

        def mod_columns(t0, t1, bank_):
            for t in range(t0, t1):
                r = mm(ps[:, bank_, t:t + 1], mod_acc[:, t, :], ones[:, 0:1], True, True, pe if t == t1 - 1 else None)
            return r

        def mod_gains(t0, t1, bank_, summed, s_):
            wait(V, summed)
            m = v_tt(mod[:, t0:t1], ps[:, bank_, t0:t1], vec[:, VEC["b_mod_2"] + t0:VEC["b_mod_2"] + t1], ALU.add)
            wait(V, m)
            g = VEC[("g_ffn1_2", "g_mix_2", "g_ffn2_2")[s_]]
            sc = mod[:, (3 * s_ + 1) * KC:(3 * s_ + 2) * KC]
            v_stt(gains[:, s_ * KC:(s_ + 1) * KC], sc, 1.0, vec[:, g:g + KC], ALU.add, ALU.mult)
            ga = mod[:, (3 * s_ + 2) * KC:(3 * s_ + 3) * KC]
            return v_ts(gains[:, (3 + s_) * KC:(4 + s_) * KC], ga, 1.0, ALU.add, 0.5 if s_ != 1 else 1.0, ALU.mult)

        M1, M2, M3 = 36, 48, 60
        mod_sum1 = mod_columns(0, M1, 6)
        rstd_done = root(AUX, EPS1, total, D_MODEL)
        wait(V, rstd_done)
        wait(V, total)
        sums = sum_squares(lambda c: v_stt(x[:, c, :], x[:, c, :], vcol("norm_final_w", c), rstd[:, :], ALU.mult, ALU.mult))

        gains_done = mod_gains(0, M1, 6, mod_sum1, 0)

        def shift_of(s):
            return lambda c: mod[:, 3 * s * KC + c:3 * s * KC + c + 1]

        def gain_of(s):
            return lambda c: gains[:, s * KC + c:s * KC + c + 1]

        def factor_of(s):
            return lambda c: col(gains, (3 + s) * KC + c) if isinstance(c, int) else col(gains, c + (3 + s) * KC)

        wait(V, gains_done)
        wait(A, gains_done)
        ready = norm(gain_of(0), shift_of(0), EPS2, sums, lambda: mod_columns(M1, M2, 5))
        mod_gains(M1, M2, 5, now(pe), 1)
        sums = ffn(ready, ((d["w1_gate_2"][0], 0), (d["w1_up_2"][0], 0)), glu_hidden, d["w1_down_2"][0], factor_of(0))
        mod_columns(M2, M3, 4)
        ready = norm(gain_of(1), shift_of(1), EPS2, sums, lambda: mod_columns(M3, MOD_TILES, 4))
        mod_sum = now(pe)
        mod_gains(M2, MOD_TILES, 4, mod_sum, 2)
        for t in (q_hi, q_lo, v_hi, v_lo):
            wait(G, mod_sum)
            zeros_set = memset(G, f32(t[:]), 0.0, pool)
        w2 = d["w_in_2"][0]

        wait(A, mod_sum)

        def project(cols, q_dst, k_dst, v_dst, ready=None, front=None, behind=None):
            ev = {}
            for s, (name, n_k, k0) in enumerate((("q", KC, 0), ("k", KC, 0), ("v", KC // 2, 0), ("v", KC // 2, KC // 2))):
                if front:
                    front(s, ev)
                b, done = unit(strip(w2, lambda i, c0=IN2[cols + name]: i * P + c0, k0, n_k), u_act, n_k=n_k, k0=k0,
                               part=None if name != "v" else k0 // (KC // 2),
                               bank=ev["v_bank"] if k0 else None, ready=ready if s == 0 else None)
                if s == 0:
                    wait(A, done)
                    ev["q"] = copy(A, lambda i: one(q_dst, i), bank(b), bank_free[b])
                elif s == 1:
                    wait(V, done)
                    ev["k"] = copy(V, lambda i: one(k_dst, i), bank(b), bank_free[b])
                elif s == 2:
                    ev["v_bank"] = b
                else:
                    v_t = t_a[0][:, 2:2 + SEQ]
                    wait(A, done)
                    t = copy(A, v_t, bank(b), bank_free[1 - b])
                    if behind:
                        behind(ev)
                    wait(T, t)
                    for tb in range(TB):
                        t = transpose(ps[:, b, tb * P:(tb + 1) * P], v_t[:, tb * P:(tb + 1) * P], P, pe)
                    wait(A, t)
                    ev["v"] = copy(A, lambda i: one(v_dst, i), bank(b), bank_free[b])
            return ev

        b, done = unit(strip(w2, IN2["ff"] + N_FOX - P), u_act, ready=ready)
        wait(A, done)
        wait(A, now(dve))
        t = copy(A, t_b[0][:, :], bank(b), bank_free[b])
        wait(T, t)
        F_BANK, NF = 6, TB * N_FOX
        for tb in range(TB):
            f = transpose(ps[:, F_BANK, tb * P:(tb + 1) * P], t_b[0][:, tb * P:(tb + 1) * P], P, pe)
        fa, fe, fl = (att_a[:, n * NF:(n + 1) * NF] for n in range(3))
        wait(V, f)
        fs = v_tt(fa.rearrange("p (t n) -> p t n", n=N_FOX), bank(F_BANK).rearrange("p (t n) -> p t n", n=P)[:, :, P - N_FOX:P],
                  bf_c[:, :].unsqueeze(1).broadcast_to([P, TB, N_FOX]), ALU.add)
        do(A, lambda e, i: e.preload_act_table_set(LN_EXP))
        wait(A, fs)
        a_fn(fe, fa, ACT.Abs)
        wait(A, now(act))
        a_fn(fe, fe, ACT.Exp, scale=-1.0)
        wait(A, now(act))
        ln = a_fn(fe, fe, ACT.Ln, bias=1.0)
        wait(V, ln)
        lf = v_stt(fl, fa, 0.0, fe, ALU.min, ALU.subtract)

        with rounds(4):
            sb_ev = project("s", sq, sk, sv)

        wait(T, lf)

        for tb in range(TB):
            dst = ps[:, F_BANK, tb * N_FOX:(tb + 1) * N_FOX]
            for t in range(tb + 1):
                f = mm(dst, consts[:, C_TRIU:C_TRIU + P] if t == tb else ones[:, :], fl[:, t * N_FOX:(t + 1) * N_FOX],
                       t == 0, t == tb, pe if t == tb else None)
        wait(V, f)
        f_done = copy(V, f_col[:, :, :], ps[:, F_BANK, 0:NF].rearrange("p (t n) -> p t n", n=N_FOX), dve)
        wait(T, f_done)
        for tb in range(TB):
            f = transpose(ps[0:N_FOX, 5, tb * P:(tb + 1) * P], f_col[:, tb, :], P, pe)
        wait(A, f)
        nh = a_fn(nf_hi[:, :], ps[0:N_FOX, 5, :], ACT.Copy, scale=-1.0)
        wait(V, nh)
        nf_done = v_stt(nf_lo[:, :], ps[0:N_FOX, 5, :], -1.0, f32(nf_hi[:, :]), ALU.mult, ALU.subtract)
        for t in (f_hi, f_lo):
            wait(G, mod_sum)
            f_zero = memset(G, f32(t[:]), 0.0, pool)

        def tri(banks, j):
            return ps[:, banks[TRI_BANK[j]], TRI_COL[j]:TRI_COL[j] + TRI_N[j]]

        def packed(banks):
            return [(banks[b], at, n) for b, at, n in PACKED]

        def tri_values(n, p_cut, v_cut, out_bank=O_BANK):
            wait(T, v_cut)
            for j in range(TB):
                wait(T, p_cut[TRI_BANK[j]])
                at = slice(TRI_OFF[j], TRI_OFF[j] + TRI_N[j])
                o = three(ps[:, out_bank, j * P:SEQ], (v_hi[:, j, n, :], v_lo[:, j, n, :]), (p_hi[:, at], p_lo[:, at]),
                          n == 0 and j == 0, True, pe if j == TB - 1 else None, skip=True)
            return o

        SB_BANKS = ((2, 3, 4), (5, 6, 7))
        SB_OUT = SB_BANKS[0][0]
        att = (att_a, att_b)

        def sb_scores(n, k_cut):
            wait(T, k_cut)
            for j in range(TB):
                js = slice(j * P, (j + 1) * P)
                s = three(tri(SB_BANKS[n], j), (k_hi[:, js], k_lo[:, js]), (q_hi[:, n, j * P:SEQ], q_lo[:, n, j * P:SEQ]),
                          j < 3, True, pe if j == TB - 1 else None, skip=j == 3)
            return s

        def sb_keep(n, scores):
            a = att[n]
            wait(A, scores)
            for b, at, w in packed(SB_BANKS[n]):
                a_fn(a[:, at:at + w], ps[:, b, 0:w], ACT.Abs)
            wait(A, now(act))
            a_fn(a[:, :], a[:, :], ACT.Exp, scale=-1.0)
            wait(A, now(act))
            ln = a_fn(a[:, :], a[:, :], ACT.Ln, bias=1.0)
            wait(V, ln)
            for b, at, w in packed(SB_BANKS[n]):
                r = v_stt(a[:, at:at + w], ps[:, b, 0:w], 0.0, a[:, at:at + w], ALU.max, ALU.add)
            wait(G, r)
            for j in range(TB):
                blk = a[:, TRI_OFF[j]:TRI_OFF[j] + P]
                r = do(G, lambda e, i, blk=blk: e.affine_select(out=blk, in_=blk, compare_op=ALU.is_gt, fill=0.0, base=0,
                                                                pattern=[[1, P]], channel_multiplier=-1), pool)
            return r

        def sb_cut(n, done):
            cuts = []
            for (_, at, w), d_ in zip(PACKED, done):
                wait(V, d_)
                h = copy(V, p_hi[:, at:at + w], att[n][:, at:at + w], dve)
                wait(V, h)
                cuts.append(v_tt(p_lo[:, at:at + w], att[n][:, at:at + w], f32(p_hi[:, at:at + w]), ALU.subtract))
            return cuts

        def sb_later(n, p_cut):
            for t in range(TB):
                wait(T, p_cut[TRI_BANK[t]])
                for j in range(t + 1):
                    dst = tri(SB_BANKS[n], j)[:, (t - j) * P:]
                    for pp in (p_hi, p_lo):
                        mm(dst, (tri_neg if t == j else ones_neg)[:, :], pp[:, TRI_OFF[t]:TRI_OFF[t] + TRI_N[t]], False, skip=True)
            for j in range(TB):
                r = mm(tri(SB_BANKS[n], j)[:, 0:P], ident_r[:, :], mask_win[:, 0:P], False, sig=pe if j == TB - 1 else None, skip=True)
            return r

        def sb_weights(n, later):
            wait(A, later)
            return sb_cut(n, [a_fn(att[n][:, at:at + w], ps[:, b, 0:w], ACT.Exp) for b, at, w in packed(SB_BANKS[n])])

        def take_output(o, dst, out_bank=O_BANK):
            wait(A, o)
            return copy(A, dst, bank(out_bank), act)

        sb_sources = (sb_ev["q"], sb_ev["k"], sb_ev["v"])
        wait(T, nf_done)

        def head_square(src, c, done):
            wait(A, done)
            wait(A, now(dve))
            return a_fn(t_b[c][:, :], lambda i: one(src, i), ACT.Square)

        def sb_front(s, ev):
            if s == 0:
                ev["kc"], ev["vc"] = stage(lambda i: one(sq, i), lambda i: one(sk, i),
                                           lambda i, n: one(sv, i).rearrange("p (t n) -> p t n", n=P)[:, :, n * HEAD_DIM:(n + 1) * HEAD_DIM],
                                           sb_sources)
            if s == 1:
                scores = sb_scores(0, ev["kc"]), sb_scores(1, ev["kc"])
                ev["p"] = sb_cut(0, [sb_keep(0, scores[0])] * len(PACKED))
                ev["scores1"] = scores[1]
            if s == 2:
                ev["p1"] = sb_keep(1, ev["scores1"])
                ev["q2"] = head_square(fq, 0, ev["q"])
            if s == 3:
                ev["w"] = sb_weights(0, sb_later(0, ev["p"]))
                ev["k2"] = head_square(fk, 1, ev["k"])

        def sb_behind(ev):
            o = tri_values(0, ev["w"], ev["vc"], SB_OUT)
            wait(V, o)
            ev["p"] = sb_cut(1, [ev["p1"]] * len(PACKED))
            wait(T, ev["q2"])
            wait(T, ev["k2"])
            for c in range(2):
                ev["s2"] = mm(bank(SB_BANKS[0][1 + c]), consts[:, C_HEADS:C_HEADS + P], t_b[c][:, :], True, True, pe)

        with rounds(4):
            ev = project("f", fq, fk, fv, front=sb_front, behind=sb_behind)
            later = sb_later(1, ev["p"])
            wait(A, ev["s2"])
            for c in range(2):
                a_fn(t_b[c][:, :], bank(SB_BANKS[0][1 + c]), ACT.Ln, bias=eps_col(EPS2), scale=1.0 / HEAD_DIM)
            wait(A, now(act))
            for c in range(2):
                r = a_fn(t_b[c][:, :], t_b[c][:, :], ACT.Exp, scale=-0.5)
            w = sb_weights(1, later)
            o = tri_values(1, w, ev["vc"], SB_OUT)
            take_output(o, lambda i: one(sq, i), SB_OUT)
            wait(V, r)
            for c, (dst, g) in enumerate(((fq, "g_q_2"), (fk, "g_k_2"))):
                fox_normed = v_stt(lambda i, t=dst: one(t, i), lambda i, t=dst: one(t, i), vcol(g, lambda i: i), t_b[c][:, :],
                                   ALU.mult, ALU.mult)

        FOX_BANKS = ((2, 3, 4), (5, 6, 1))
        fox_sources = (fox_normed, ev["q"], ev["v"], nf_done, f_zero)

        def fox_scores(n):
            for b in reversed(range(TB)):
                reg, bs, w = tri(FOX_BANKS[n], TB - 1 - b), slice(b * P, (b + 1) * P), (b + 1) * P
                three(reg, (q_hi[:, n, bs], q_lo[:, n, bs]), (k_hi[:, 0:w], k_lo[:, 0:w]), True, False)
                mm(reg, ones_r[:, :], f_hi[:, n, 0:w], False, False)
                mm(reg, ones_r[:, :], f_lo[:, n, 0:w], False, False)
                s = mm(reg[:, b * P:w], ident_r[:, :], mask_win[:, P:2 * P], False, True, pe if b == 0 else None)
            return s

        def fox_exp(n, pair, scores, buf):
            c0 = 4 + 16 * n
            mx, nm, den = (small[:, c0 + 4 * t:c0 + 4 * t + 4] for t in range(3))
            gate = lambda i: f_col[:, :, span(pair(i) * 2 + n, 1)].squeeze(2)
            wait(V, scores)
            for b in range(TB):
                do(V, lambda e, i, b=b: e.tensor_reduce(mx[:, b:b + 1], tri(FOX_BANKS[n], TB - 1 - b), AX_X, ALU.max), dve)
            wait(V, now(dve))
            v_tt(mx, mx, gate, ALU.add)
            wait(V, now(dve))
            r = v_tt(nm, gate, mx, ALU.subtract)
            wait(A, r)
            for b in range(TB):
                j = TB - 1 - b
                ex = a_fn(buf[:, TRI_OFF[j]:TRI_OFF[j] + TRI_N[j]], tri(FOX_BANKS[n], j), ACT.Exp, bias=nm[:, b:b + 1],
                          accum=den[:, b:b + 1])
            return ex

        def fox_divide(n, ex, buf):
            den = small[:, 12 + 16 * n:16 + 16 * n]
            wait(V, ex)
            rc = do(V, lambda e, i: e.reciprocal(den, den), dve)
            wait(V, rc)
            for b in range(TB):
                w = buf[:, TRI_OFF[TB - 1 - b]:TRI_OFF[TB - 1 - b] + TRI_N[TB - 1 - b]]
                r = v_ts(w, w, den[:, b:b + 1], ALU.mult)
            return r

        def fox_transpose(n, probs, buf):
            wait(T, probs)
            for j in range(TB):
                for b in range(j, TB):
                    at = TRI_OFF[TB - 1 - b] + j * P
                    t = transpose(tri(FOX_BANKS[n], j)[:, (b - j) * P:(b - j + 1) * P], buf[:, at:at + P], P, pe)
            return t

        def fox_stage(pair, scored):
            wait(A, scored)
            wait(G, scored)
            for n in range(2):
                for t, src in ((f_hi, nf_hi), (f_lo, nf_lo)):
                    v_tt(t[0:N_FOX, n, :], f32(src[:, :]), lambda i, n=n: consts[0:N_FOX, span(
                        pair(i) * 2 + (C_IDENT + n), 1)].broadcast_to([N_FOX, SEQ]), ALU.mult, pool, G)
            stage_q_k(lambda i: one(fq, pair(i)), lambda i: one(fk, pair(i)))

        def fox_pair(pair, more):
            staged = now(dve), now(pool)
            wait(A, now(pe))
            vc = stage_v(lambda i, n: one(fv, pair(i)).rearrange("p (t n) -> p t n", n=P)[:, :, n * HEAD_DIM:(n + 1) * HEAD_DIM])
            wait(T, *staged)
            s0 = fox_scores(0)
            s1 = fox_scores(1)
            e0 = fox_exp(0, pair, s0, att_a)
            e1 = fox_exp(1, pair, s1, att_b)
            t0 = fox_transpose(0, fox_divide(0, e0, att_a), att_a)
            p1 = fox_divide(1, e1, att_b)
            c0 = cut_from_banks(packed(FOX_BANKS[0]), t0)
            fox_transpose(1, p1, att_b)
            o = tri_values(0, c0, vc)
            c1 = cut_from_banks(packed(FOX_BANKS[1]), o)
            o = tri_values(1, c1, vc)
            if more:
                fox_stage(lambda i: pair(i) + 1, s1)
            return take_output(o, lambda i: one(fq, pair(i)))

        wait(A, *fox_sources)
        wait(V, *fox_sources)
        wait(G, *fox_sources)
        fox_stage(lambda i: 0, now(pe))
        with rounds(3):
            fox_pair(lambda i: i, True)
        fox_out = fox_pair(lambda i: 3, False)

        ready = {}
        for c in range(KC):
            src = (sq if c < KC // 2 else fq)[:, c % (KC // 2), :]
            wait(A, fox_out)
            h = copy(A, u_hi[:, c, :], src, act)
            wait(V, h)
            ready[c] = v_tt(u_lo[:, c, :], src, f32(u_hi[:, c, :]), ALU.subtract)
        clear_ssum()
        sums = residual(d["w_o_2"][0], u_act, ready, factor_of(1), squares=True)

        ready = norm(gain_of(2), shift_of(2), EPS2, sums)
        out_tok = out[0].rearrange("(t p) n -> p t n", p=P)

        def write_out(c, done):
            wait(T, done)
            b = 2 + c % 4
            for tb in range(TB):
                t = transpose(ps[:, b, tb * P:(tb + 1) * P], x[:, c, tb * P:(tb + 1) * P], P, pe)
            dst = (sq if c < KC // 2 else sk)[:, c % (KC // 2), :]
            wait(A, t)
            r = copy(A, dst, bank(b), act)
            wait(G, r)
            dma(G, out_tok[:, :, c * P:(c + 1) * P], dst.rearrange("p (t n) -> p t n", n=P), out_written)

        ffn(ready, ((d["w2_gate_2"][0], 0), (d["w2_up_2"][0], 0)), glu_hidden, d["w2_down_2"][0], factor_of(2), after=write_out)
        wait(G, now(out_written))

        with nc.Block() as block:
            block.sync(lambda e: pr.run(S, e))
            block.scalar(lambda e: pr.run(A, e))
            block.vector(lambda e: pr.run(V, e))
            block.gpsimd(lambda e: pr.run(G, e))
            block.tensor(lambda e: pr.run(T, e))


NAMES = ("x", "positions", "norm_mix_w", "w_in", "b_in", "conv_mix_w", "w_conv_out", "w_attn_out", "b_attn_out",
         "sinks", "w_mix_out", "norm_ffn_w", "w_ffn_up", "ffn_conv_w", "ffn_conv_b", "w_ffn_down", "norm_final_w",
         "c_2", "w_mod_2", "b_mod_2", "g_ffn1_2", "w1_gate_2", "w1_up_2", "w1_down_2", "g_mix_2", "w_in_2", "b_f_2",
         "g_q_2", "g_k_2", "w_o_2", "g_ffn2_2", "w2_gate_2", "w2_up_2", "w2_down_2")


def kernel(**inputs):
    import concourse.bacc as bacc
    from concourse.bass_utils import run_bass_kernel_spmd

    nc = bacc.Bacc("TRN2", target_bir_lowering=False, num_devices=1)
    arrays = {name: np.ascontiguousarray(inputs[name]) for name in NAMES} | {"consts": constants()}
    arrays = {"in_" + n: a for n, a in arrays.items()}
    d = {n[3:]: nc.dram_tensor(n, a.shape, mybir.dt.from_np(a.dtype), kind="ExternalInput").ap() for n, a in arrays.items()}
    out = nc.dram_tensor("out", (1, SEQ, D_MODEL), F32, kind="ExternalOutput").ap()
    two_blocks(nc, d, out)
    return run_bass_kernel_spmd(nc, [arrays], core_ids=[0]).results[0]["out"]
```
